# Optimizing a Trainium2 kernel written in Bass

```python
import math
import jax
import jax.numpy as jnp
from jax import lax
import numpy as np

D_MODEL = 1024
BATCH = 1
SEQ = 256
DEPTH = 1

HEAD_DIM = 64
HEADS_PER_GROUP = 4
ATTN_GROUPS = ((128, 1), (512, 4), (2048, 16))
N_ATTN_HEADS = HEADS_PER_GROUP * len(ATTN_GROUPS)
ATTN_WIDTH = N_ATTN_HEADS * HEAD_DIM
ATTN_OUT_WIDTH = HEADS_PER_GROUP * HEAD_DIM
ROPE_THETA = 10000.0
SSM_WIDTH = D_MODEL // 2
SSM_GROUP = 16
SSM_GROUPS = SSM_WIDTH // SSM_GROUP
SSM_STATE = 64
DT_MIN = 0.001
DT_MAX = 0.1
N_BRANCHES = 2
IN_WIDTH = 3 * ATTN_WIDTH + SSM_WIDTH + N_BRANCHES * D_MODEL
N_EXPERTS = 32
TOP_K = 4
D_EXPERT = D_MODEL
SWIGLU_ALPHA = 1.702
SWIGLU_LIMIT = 7.0
MOE_BLOCK = 256
NORM_EPS = 1e-6
MASK_VALUE = -1e30

kernel_name = 'hybrid_dilated_attn_s5_moe_block'

def _rmsnorm(x, gain):
    x32 = x.astype(jnp.float32)
    y = x32 * lax.rsqrt(jnp.mean(x32 * x32, axis=-1, keepdims=True) + NORM_EPS)
    return (y * gain.astype(jnp.float32)).astype(x.dtype)

def _rope(t):
    seq, dh = t.shape[1], t.shape[-1]
    inv_freq = ROPE_THETA ** (-jnp.arange(0, dh, 2, dtype=jnp.float32) / dh)
    ang = jnp.arange(seq, dtype=jnp.float32)[:, None] * inv_freq[None, :]
    cos = jnp.cos(ang)[None, :, None, :]
    sin = jnp.sin(ang)[None, :, None, :]
    t32 = t.astype(jnp.float32)
    t1, t2 = t32[..., : dh // 2], t32[..., dh // 2:]
    return jnp.concatenate([t1 * cos - t2 * sin, t2 * cos + t1 * sin], axis=-1).astype(t.dtype)

def _banded_attention(q, k, v, half):
    n, length, heads, dh = q.shape
    nb = -(-length // half)
    pad = nb * half - length
    qb = jnp.pad(q, ((0, 0), (0, pad), (0, 0), (0, 0))).reshape(n, nb, half, heads, dh)

    def windows(t):
        tp = jnp.pad(t, ((0, 0), (half, pad + half), (0, 0), (0, 0))).reshape(n, nb + 2, half, heads, dh)
        return jnp.concatenate([tp[:, :-2], tp[:, 1:-1], tp[:, 2:]], axis=2)

    kw = windows(k)
    vw = windows(v)
    scores = jnp.einsum('nbqhd,nbkhd->nbhqk', qb, kw).astype(jnp.float32) * (dh ** -0.5)
    blk = jnp.arange(nb)[:, None]
    qpos = blk * half + jnp.arange(half)[None, :]
    kpos = (blk - 1) * half + jnp.arange(3 * half)[None, :]
    rel = kpos[:, None, :] - qpos[:, :, None]
    valid = (jnp.abs(rel) <= half) & (kpos[:, None, :] >= 0) & (kpos[:, None, :] < length)
    scores = jnp.where(valid[None, :, None], scores, MASK_VALUE)
    m = jnp.max(scores, axis=-1, keepdims=True)
    p = jnp.exp(scores - m)
    denom = jnp.sum(p, axis=-1)
    o = jnp.einsum('nbhqk,nbkhd->nbqhd', p, vw.astype(jnp.float32)) / jnp.swapaxes(denom, 2, 3)[..., None]
    lse = jnp.swapaxes(m[..., 0] + jnp.log(denom), 2, 3)
    o = o.reshape(n, nb * half, heads, dh)[:, :length]
    lse = lse.reshape(n, nb * half, heads)[:, :length]
    return o, lse

def _dilated_group(q, k, v, window, dilation):
    bsz, seq, heads, dh = q.shape
    length = seq // dilation
    half = window // (2 * dilation)

    def split(t):
        return t.reshape(bsz, length, dilation, heads, dh).transpose(0, 2, 1, 3, 4).reshape(bsz * dilation, length, heads, dh)

    o, lse = _banded_attention(split(q), split(k), split(v), half)
    o = o.reshape(bsz, dilation, length, heads, dh).transpose(0, 2, 1, 3, 4).reshape(bsz, seq, heads, dh)
    lse = lse.reshape(bsz, dilation, length, heads).transpose(0, 2, 1, 3).reshape(bsz, seq, heads)
    return o, lse

def _dilated_attention_mixer(q, k, v):
    bsz, seq = q.shape[0], q.shape[1]
    outs = []
    lses = []
    for g, (window, dilation) in enumerate(ATTN_GROUPS):
        sl = slice(g * HEADS_PER_GROUP, (g + 1) * HEADS_PER_GROUP)
        o, lse = _dilated_group(q[:, :, sl], k[:, :, sl], v[:, :, sl], window, dilation)
        outs.append(o)
        lses.append(lse)
    o = jnp.stack(outs)
    weights = jax.nn.softmax(jnp.stack(lses), axis=0)
    y = jnp.sum(weights[..., None] * o, axis=0)
    return y.reshape(bsz, seq, ATTN_OUT_WIDTH).astype(q.dtype)

def _complex_linear_combine(e1, e2):
    a1r, a1i, b1r, b1i = e1
    a2r, a2i, b2r, b2i = e2
    ar = a2r * a1r - a2i * a1i
    ai = a2r * a1i + a2i * a1r
    br = a2r * b1r - a2i * b1i + b2r
    bi = a2r * b1i + a2i * b1r + b2i
    return (ar, ai, br, bi)

def _s5_mixer(u, lam_re, lam_im, log_dt, b_re, b_im, c_re, c_im, d_skip, w_glu, b_glu):
    bsz, seq, _ = u.shape
    ug = u.reshape(bsz, seq, SSM_GROUPS, SSM_GROUP).astype(jnp.float32)
    y = d_skip.astype(jnp.float32) * ug
    for direction in range(2):
        lr = lam_re[direction].astype(jnp.float32)
        li = lam_im[direction].astype(jnp.float32)
        dt = jnp.exp(log_dt[direction].astype(jnp.float32))[:, None]
        mag = jnp.exp(lr * dt)
        ab_re = mag * jnp.cos(li * dt)
        ab_im = mag * jnp.sin(li * dt)
        den = lr * lr + li * li
        nr = ab_re - 1.0
        f_re = (nr * lr + ab_im * li) / den
        f_im = (ab_im * lr - nr * li) / den
        bu_re = jnp.einsum('bsgc,gpc->bsgp', ug, b_re[direction].astype(jnp.float32))
        bu_im = jnp.einsum('bsgc,gpc->bsgp', ug, b_im[direction].astype(jnp.float32))
        x_re = f_re * bu_re - f_im * bu_im
        x_im = f_re * bu_im + f_im * bu_re
        a_re = jnp.broadcast_to(ab_re, x_re.shape)
        a_im = jnp.broadcast_to(ab_im, x_im.shape)
        _, _, s_re, s_im = lax.associative_scan(_complex_linear_combine, (a_re, a_im, x_re, x_im), axis=1, reverse=(direction == 1))
        y = y + jnp.einsum('bsgp,gcp->bsgc', s_re, c_re[direction].astype(jnp.float32)) - jnp.einsum('bsgp,gcp->bsgc', s_im, c_im[direction].astype(jnp.float32))
    z = jax.nn.gelu(y.reshape(bsz, seq, SSM_WIDTH)).astype(u.dtype)
    return z * jax.nn.sigmoid(z @ w_glu + b_glu)

def _moe(h, w_router, b_router, w_gate_up, b_gate_up, w_down, b_down):
    bsz, seq, d = h.shape
    t = bsz * seq
    xt = h.reshape(t, d)
    logits = (xt @ w_router + b_router).astype(jnp.float32)
    top_vals, top_idx = lax.top_k(logits, TOP_K)
    gate_w = jax.nn.softmax(top_vals, axis=-1)
    e_flat = top_idx.reshape(-1)
    w_flat = gate_w.reshape(-1)
    tok = jnp.repeat(jnp.arange(t, dtype=jnp.int32), TOP_K)
    order = jnp.argsort(e_flat)
    e_sorted = e_flat[order]
    counts = jnp.bincount(e_flat, length=N_EXPERTS)
    padded = ((counts + MOE_BLOCK - 1) // MOE_BLOCK) * MOE_BLOCK
    pad_end = jnp.cumsum(padded)
    pad_start = pad_end - padded
    start = jnp.cumsum(counts) - counts
    rank = jnp.arange(t * TOP_K) - start[e_sorted]
    dest = pad_start[e_sorted] + rank
    n_rows = (-(-(t * TOP_K) // MOE_BLOCK) + N_EXPERTS) * MOE_BLOCK
    n_blocks = n_rows // MOE_BLOCK
    row_tok = jnp.full((n_rows,), t, dtype=jnp.int32).at[dest].set(tok[order])
    row_w = jnp.zeros((n_rows,), dtype=h.dtype).at[dest].set(w_flat[order].astype(h.dtype))
    block_exp = jnp.minimum(jnp.searchsorted(pad_end, jnp.arange(n_blocks) * MOE_BLOCK, side='right'), N_EXPERTS - 1)
    x_pad = jnp.concatenate([xt, jnp.zeros((1, d), xt.dtype)], axis=0)
    xs = x_pad[row_tok].reshape(n_blocks, MOE_BLOCK, d)

    def expert_block(args):
        xb, e = args
        gu = xb @ w_gate_up[e] + b_gate_up[e]
        gate, up = gu[:, :D_EXPERT], gu[:, D_EXPERT:]
        gate = jnp.minimum(gate, SWIGLU_LIMIT)
        up = jnp.clip(up, -SWIGLU_LIMIT, SWIGLU_LIMIT)
        act = gate * jax.nn.sigmoid(SWIGLU_ALPHA * gate) * (up + 1.0)
        return act @ w_down[e] + b_down[e]

    ys = lax.map(expert_block, (xs, block_exp)).reshape(n_rows, d)
    out = jnp.zeros((t + 1, d), h.dtype).at[row_tok].add(ys * row_w[:, None])[:t]
    return out.reshape(bsz, seq, d)

def setup_inputs(seed: int = 0) -> dict:
    key = jax.random.key(seed)
    ks = jax.random.split(key, 26)
    f32 = jnp.float32
    G, P, C = SSM_GROUPS, SSM_STATE, SSM_GROUP

    def nrm(k, shape, scale):
        return jax.random.normal(k, shape, f32) * scale

    return {
        'x': nrm(ks[0], (BATCH, SEQ, D_MODEL), 1.0),
        'norm1': 1.0 + nrm(ks[1], (DEPTH, D_MODEL), 0.02),
        'w_in': nrm(ks[2], (DEPTH, D_MODEL, IN_WIDTH), D_MODEL ** -0.5),
        'q_norm': 1.0 + nrm(ks[3], (DEPTH, N_ATTN_HEADS, HEAD_DIM), 0.02),
        'k_norm': 1.0 + nrm(ks[4], (DEPTH, N_ATTN_HEADS, HEAD_DIM), 0.02),
        'lam_re': -0.5 * jnp.exp(nrm(ks[5], (DEPTH, 2, G, P), 0.05)),
        'lam_im': jnp.pi * jnp.arange(P, dtype=f32) + nrm(ks[6], (DEPTH, 2, G, P), 0.01),
        'log_dt': jax.random.uniform(ks[7], (DEPTH, 2, G), f32, math.log(DT_MIN), math.log(DT_MAX)),
        'b_re': nrm(ks[8], (DEPTH, 2, G, P, C), (2 * C) ** -0.5),
        'b_im': nrm(ks[9], (DEPTH, 2, G, P, C), (2 * C) ** -0.5),
        'c_re': nrm(ks[10], (DEPTH, 2, G, C, P), P ** -0.5),
        'c_im': nrm(ks[11], (DEPTH, 2, G, C, P), P ** -0.5),
        'd_skip': nrm(ks[12], (DEPTH, G, C), 1.0),
        'w_glu': nrm(ks[13], (DEPTH, SSM_WIDTH, SSM_WIDTH), SSM_WIDTH ** -0.5),
        'b_glu': nrm(ks[14], (DEPTH, SSM_WIDTH), 0.01),
        'w_attn_branch': nrm(ks[15], (DEPTH, ATTN_OUT_WIDTH, D_MODEL), ATTN_OUT_WIDTH ** -0.5),
        'w_ssm_branch': nrm(ks[16], (DEPTH, SSM_WIDTH, D_MODEL), SSM_WIDTH ** -0.5),
        'w_out': nrm(ks[17], (DEPTH, D_MODEL, D_MODEL), D_MODEL ** -0.5),
        'norm2': 1.0 + nrm(ks[18], (DEPTH, D_MODEL), 0.02),
        'w_router': nrm(ks[19], (DEPTH, D_MODEL, N_EXPERTS), D_MODEL ** -0.5),
        'b_router': nrm(ks[20], (DEPTH, N_EXPERTS), 0.01),
        'w_gate_up': nrm(ks[21], (DEPTH, N_EXPERTS, D_MODEL, 2 * D_EXPERT), D_MODEL ** -0.5),
        'b_gate_up': nrm(ks[22], (DEPTH, N_EXPERTS, 2 * D_EXPERT), 0.01),
        'w_down': nrm(ks[23], (DEPTH, N_EXPERTS, D_EXPERT, D_MODEL), D_EXPERT ** -0.5),
        'b_down': nrm(ks[24], (DEPTH, N_EXPERTS, D_MODEL), 0.01),
    }

def reference(x, norm1, w_in, q_norm, k_norm, lam_re, lam_im, log_dt, b_re, b_im, c_re, c_im, d_skip, w_glu, b_glu, w_attn_branch, w_ssm_branch, w_out, norm2, w_router, b_router, w_gate_up, b_gate_up, w_down, b_down):
    bsz, seq, _ = x.shape
    o_k = ATTN_WIDTH
    o_v = 2 * ATTN_WIDTH
    o_u = 3 * ATTN_WIDTH
    o_g = o_u + SSM_WIDTH
    for l in range(DEPTH):
        h = _rmsnorm(x, norm1[l])
        proj = h @ w_in[l]
        q = proj[..., :o_k].reshape(bsz, seq, N_ATTN_HEADS, HEAD_DIM)
        k = proj[..., o_k:o_v].reshape(bsz, seq, N_ATTN_HEADS, HEAD_DIM)
        v = proj[..., o_v:o_u].reshape(bsz, seq, N_ATTN_HEADS, HEAD_DIM)
        u = proj[..., o_u:o_g]
        gates = jax.nn.sigmoid(proj[..., o_g:].astype(jnp.float32)).astype(x.dtype).reshape(bsz, seq, N_BRANCHES, D_MODEL)
        q = _rope(_rmsnorm(q, q_norm[l]))
        k = _rope(_rmsnorm(k, k_norm[l]))
        y_attn = _dilated_attention_mixer(q, k, v) @ w_attn_branch[l]
        y_ssm = _s5_mixer(u, lam_re[l], lam_im[l], log_dt[l], b_re[l], b_im[l], c_re[l], c_im[l], d_skip[l], w_glu[l], b_glu[l]) @ w_ssm_branch[l]
        mixed = gates[:, :, 0] * y_attn + gates[:, :, 1] * y_ssm
        x = x + mixed @ w_out[l]
        x = x + _moe(_rmsnorm(x, norm2[l]), w_router[l], b_router[l], w_gate_up[l], b_gate_up[l], w_down[l], b_down[l])
    return x


_drawn_inputs = setup_inputs


def setup_inputs(seed=0):
    import zlib

    import numpy as np

    out = dict(_drawn_inputs(seed))
    spreads = {}
    factors = {'q_norm': 5.321,
     'k_norm': 8.0,
     'lam_re': 5.028,
     'b_glu': 5.571,
     'b_gate_up': 8.0,
     'b_down': 8.0}
    for name, (base, spread) in spreads.items():
        noise = np.random.default_rng([zlib.crc32(name.encode()), seed]).standard_normal(out[name].shape)
        drawn = base * np.exp(spread * noise) if base else spread * noise
        out[name] = jnp.asarray(drawn.astype(out[name].dtype))
    for name, factor in factors.items():
        out[name] = (out[name] * factor).astype(out[name].dtype)
    return out
```

```python
import concourse.bass as bass
from concourse import mybir
from contextlib import ExitStack

F32 = mybir.dt.float32
BF16 = mybir.dt.bfloat16
I32 = mybir.dt.int32
U32 = mybir.dt.uint32
ALU = mybir.AluOpType
ACT = mybir.ActivationFunctionType
AXX = mybir.AxisListType.X

P = 128
SEQ = 256
TT = SEQ // P
D = 1024
KT = D // P
HD = 64
NQK = 24
QKW = NQK * HD
VW = 12 * HD
NB = 16
EXPERTS = 32
PAIRS = EXPERTS // 2
CAP = 64
PASSES = SEQ // CAP
SLOT = 2048
SLOTS = 12
PRO = 5
EPS = 1e-6
INV_2PI = 0.15915494309189535
ROUND = 12582912.0
PI_1, PI_2, PI_3 = 6.28125, 0.0019350051879882812, 3.0199159819567e-07
GELU_C, GELU_A = 0.7978845608028654, 0.044715
BIG = 1024.0


def build(nc, a, consts, out):
    ctx = ExitStack()
    with ctx:
        ring = ctx.enter_context(nc.sbuf_tensor("ring", [P, SLOTS * SLOT], F32))
        rest = ctx.enter_context(nc.sbuf_tensor("rest", [P, 28600], F32))
        cursor = {"ring": PRO * SLOT, "rest": 0}

        def sem(name):
            return ctx.enter_context(nc.semaphore(name))

        def take(store, n):
            at = cursor[store]
            cursor[store] += n
            return (ring if store == "ring" else rest)[:, at:at + n]

        def part(region, at, n):
            return region[:, at:at + n]

        banks = [ctx.enter_context(nc.psum_tensor(f"bank{i}", [P, 512], F32)) for i in range(8)]

        E = take("ring", 2 * 32 * P).rearrange("p (r k j) -> p r k j", r=2, k=32)
        masks = take("ring", TT * VW).rearrange("p (t n) -> p t n", t=TT)
        qk_gain = take("ring", QKW)
        uT = take("ring", 4 * SEQ).rearrange("p (m t) -> p m t", m=4)
        uTr = take("ring", 4 * SEQ).rearrange("p (m t) -> p m t", m=4)
        Bn_flat = take("ring", 2 * 32 * 16)
        Bn = Bn_flat.rearrange("p (r k c) -> p r k c", r=2, k=32)
        yT = Bn_flat.rearrange("p (m t) -> p m t", m=4)
        assert cursor["ring"] == SLOTS * SLOT

        hT_flat = take("rest", KT * SEQ)
        XT_flat = take("rest", 4 * 2048)
        BT_flat = take("rest", 16 * P)
        CT_flat = take("rest", 2 * 3 * 16 * 32)
        raw_flat = take("rest", TT * QKW)
        v_flat = take("rest", TT * VW)
        gT_flat = take("rest", 16 * SEQ)
        qkT_flat = take("rest", 12 * SEQ)
        atT = take("rest", 2 * SEQ).rearrange("p (m t) -> p m t", m=2)
        ident = take("rest", P)
        rope = take("rest", TT * HD).rearrange("p (t n) -> p t n", t=TT)
        PAR = take("rest", 5 * 32).rearrange("p (v k) -> p v k", v=5)
        E128 = take("rest", 2 * 32).rearrange("p (r k) -> p r k", r=2)
        small = take("rest", 400)

        hT = hT_flat.rearrange("p (k t) -> p k t", k=KT)
        X, T = [], []
        for s in range(4):
            slot = part(XT_flat, 2048 * s, 2048)
            X.append(part(slot, 0, 1024).rearrange("p (k r t) -> p k r t", k=2, r=2))
            T.append(part(slot, 1024, 1024).rearrange("p (k r t) -> p k r t", k=2, r=2))
        X4 = [part(XT_flat, 2048 * s, 1024).rearrange("p (k q j) -> p k q j", k=2, q=4) for s in range(4)]
        T4 = [part(XT_flat, 2048 * s + 1024, 1024).rearrange("p (k q j) -> p k q j", k=2, q=4) for s in range(4)]
        xs = part(XT_flat, 0, 2048).rearrange("p (t n) -> p t n", t=TT)
        BD = part(XT_flat, 2048, 2048).rearrange("p (r k g c) -> p r k g c", r=2, k=32, g=2)
        BDt = part(XT_flat, 2048, 2048).rearrange("p (n q) -> p n q", n=16)
        Cn = part(XT_flat, 4096, 2048).rearrange("p (r n u s) -> p r n u s", r=2, n=8, u=2)
        Cn_t = part(XT_flat, 4096, 2048).rearrange("p (n q) -> p n q", n=16)
        Etmp = part(XT_flat, 6144, 2048).rearrange("p (e v k j) -> p e v k j", e=2, v=2, k=16)
        BT = BT_flat.rearrange("p (n s) -> p n s", n=16)
        CT = CT_flat.rearrange("p (d v k g c) -> p d v k g c", d=2, v=3, k=16, g=2)
        raw = raw_flat.rearrange("p (t n) -> p t n", t=TT)
        probs = part(raw_flat, 0, 2 * VW).rearrange("p (b n) -> p b n", b=2)
        probsT = part(raw_flat, 2 * VW, 2 * VW).rearrange("p (n q) -> p n q", n=6)
        v = v_flat.rearrange("p (t n) -> p t n", t=TT)
        gT = gT_flat.rearrange("p (m t) -> p m t", m=16)
        PR = part(gT_flat, 0, 20 * P)[0:32, :].rearrange("p (v s) -> p v s", v=20)
        square = part(gT_flat, 20 * P, D)
        qkT = qkT_flat.rearrange("p (n t) -> p n t", n=12)
        gain1 = part(qkT_flat, 0, D)
        Btmp = part(qkT_flat, D, 1024).rearrange("p (v k c) -> p v k c", v=2, k=32)
        ss = part(small, 0, 2)
        rstd = part(small, 2, 2)
        ss_qk = part(small, 4, 24)
        rs_qk = part(small, 28, 24)
        nmax = part(small, 52, 8)
        rsum = part(small, 60, 8)
        rinv = part(small, 68, 8)
        d_col = part(small, 76, 4)
        bglu_col = part(small, 80, 4)
        ldt = part(small, 84, 4)
        carry = part(small, 88, 12)
        dt_row = part(small, 100, 2)

        YA_BANK, YS_BANK, XO_BANK = (0, 1, 6, 7), (2, 3, 4, 5), (0, 1, 6, 7)
        S = {n: sem(n) for n in (
            "x_in ident_in lam_in bc_in rope_in cols_in gain1_in gate_in x_back moe_in bias_in bias_parts "
            "sq_done std_done h_ready hT_trans hT_copy uT_done uT_copy dt_ready mag_ready rows_ready "
            "sin_ready par_trans par_ready bd_zero bd_ready bd_trans bd_copy c_trans c_copy "
            "table_fwd table_bwd ct_zero ct_ready proj_done proj_copied bu_done bu_copied rin_odd scan_done "
            "rout_even rout_odd ssm_y yf_copied qk_ms qk_std qk_ready qkT_done qkT_copied scores_done "
            "pmax_ready exp_done probs_ready pt_done pt_copied yb_ready tanh_ready z_ready glu_done "
            "sig_ready zg_ready gates_ready ya_done ys_done mixed_ready out_unit_used xo_done x1_ready "
            "dve_chain pool_chain moe_sq moe_std h2_ready h2T_done h2T_copied logit_done "
            "negmax_ready ex_ready route_ready rank_done ranks_ready wt_done wt_copied counted passes_known acc_done out_ready "
            "out_stored").split()}
        slot_full = [sem(f"slot_full{i}") for i in range(SLOTS)]
        M = {n: sem("moe_" + n) for n in (
            "onehots gathered xT gw_ready swt scatter_w up_gate half_done gmin clipped sigm act_ready act_trans actT "
            "y_low y_high unit_used iota_ready").split()}

        w_in = a["w_in"][0].rearrange("(k p) n -> p k n", p=P)
        units = []
        for half in range(2):
            units.append((w_in[:, 4 * half:4 * half + 4, 2304:2816], 512))
        for c in range(4):
            for half in range(2):
                units.append((w_in[:, 4 * half:4 * half + 4, 512 * c:512 * c + 512], 512))
        units.append((w_in[:, :, 2048:2304], 256))
        for c in range(4):
            for half in range(2):
                units.append((w_in[:, 4 * half:4 * half + 4, 2816 + 512 * c:3328 + 512 * c], 512))
        U_QKV, U_GATE = 2, 11
        U_GLU = len(units)
        units.append((a["w_glu"][0].rearrange("(k p) n -> p k n", p=P), 512))
        U_AB = len(units)
        units.append((a["w_attn_branch"][0].rearrange("(k p) n -> p k n", p=P), 1024))
        U_SB = len(units)
        w_sb = a["w_ssm_branch"][0].rearrange("(k p) n -> p k n", p=P)
        units += [(w_sb[:, 2 * i:2 * i + 2, :], 1024) for i in range(2)]
        U_OUT = len(units)
        w_o = a["w_out"][0].rearrange("(k p) n -> p k n", p=P)
        units += [(w_o[:, 2 * i:2 * i + 2, :], 1024) for i in range(4)]
        n_units = len(units)
        pro_loads = [len(range(s, n_units, PRO)) if s < PRO else 0 for s in range(SLOTS)]

        def unit(n):
            cols = units[n][1]
            s = n % PRO
            return ring[:, SLOT * s:SLOT * (s + 1)].rearrange("p (k n) -> p k n", n=cols)

        JOB_QKV = {(c, t): 2 * c + t for c in range(5) for t in range(TT)}
        JOB_GATE, JOB_PV, n_job = {}, {}, 10
        for i in range(8):
            JOB_GATE[i] = n_job
            n_job += 1
            if i % 2:
                JOB_PV[i // 2] = n_job
                n_job += 1

        freed = {}
        for n in (0, 1):
            freed[n] = (S["uT_done"], 2)
        for c in range(5):
            for n in ((U_QKV + 2 * c, U_QKV + 2 * c + 1) if c < 4 else (U_QKV + 8,)):
                freed[n] = (S["proj_done"], JOB_QKV[c, 1] + 1)
        for c in range(4):
            for n in (U_GATE + 2 * c, U_GATE + 2 * c + 1):
                freed[n] = (S["proj_done"], JOB_GATE[2 * c + 1] + 1)
        freed[U_GLU] = (S["glu_done"], 2)
        freed[U_AB] = (S["ya_done"], 4)
        freed[U_SB] = freed[U_SB + 1] = (S["ys_done"], 4)
        for i in range(3):
            freed[U_OUT + i] = (S["out_unit_used"], i + 1)
        freed[U_OUT + 3] = (S["xo_done"], 4)

        steps = [("bu", b) for b in range(4)]
        for j in range(18):
            if j < 10:
                steps.append(("qkv", j // 2, j % 2))
            else:
                i = j - 10
                steps += [("scores", i), ("gate", i), ("pt", i)]
                if i % 2:
                    steps.append(("pv", i // 2))
            if j >= 2:
                steps.append(("y", j - 2))
                if j + 2 < NB:
                    steps.append(("bu", j + 2))
                if j in (5, 6):
                    steps.append(("qk_std", j - 5))
        first_scores = steps.index(("scores", 0))
        steps[first_scores:first_scores] = [("qkT", 0), ("qkT", 1)]

        def tiles(b):
            return b // 8, (2 * (b % 8), 2 * (b % 8) + 1)

        x1 = hT_flat.rearrange("p (t n) -> p t n", t=TT)
        h2 = BT_flat.rearrange("p (t n) -> p t n", t=TT)
        h2T = part(XT_flat, 0, 2048).rearrange("p (k t) -> p k t", k=KT)
        mT = part(XT_flat, 5120, 2048).rearrange("p (k t) -> p k t", k=KT)
        z_tmp = part(XT_flat, 0, 1024).rearrange("p (m t) -> p m t", m=4)
        z_th = part(XT_flat, 1024, 1024).rearrange("p (m t) -> p m t", m=4)
        z = part(XT_flat, 2048, 1024).rearrange("p (m t) -> p m t", m=4)
        z_sig = part(XT_flat, 3072, 1024).rearrange("p (m t) -> p m t", m=4)
        zg = part(XT_flat, 4096, 1024).rearrange("p (m t) -> p m t", m=4)

        cursor["moe"] = 0
        moe_flat = rest[:, 2048 + 8192 + 2048:2048 + 8192 + 2048 + 3072 + 3072]

        def moe(n):
            at = cursor["moe"]
            cursor["moe"] += n
            assert cursor["moe"] <= 6144
            return moe_flat[:, at:at + n]

        bgu = moe(2048)[0:96, :]
        bgu3 = moe(1024)[0:96, :].bitcast(BF16)
        bgu_t = moe(1024)[0:96, :].bitcast(BF16)
        bdn = moe(1024)[0:32, :]
        wr = moe(256).rearrange("p (k e) -> p k e", k=KT)
        tri = moe(P)
        pick = moe(48)[0:96, :]
        XeT = part(XT_flat, 2048, 512).rearrange("p (k r) -> p k r", k=KT)
        acT = part(XT_flat, 2560, 512).rearrange("p (k r) -> p k r", k=KT)
        ysb = part(XT_flat, 3072, 1024)
        SW = part(XT_flat, 4096, SEQ)
        gain2 = part(v_flat, 0, D)
        iota2 = part(v_flat, D, CAP)
        iota32 = part(v_flat, D + P, 32)
        ones = part(v_flat, D + P + 32, P)
        G = part(qkT_flat, 0, 128).rearrange("p (t r) -> p t r", t=TT)
        GW = part(qkT_flat, 128, 256).rearrange("p (t u r) -> p t u r", t=TT, u=2)
        sel = part(qkT_flat, 384, 32)[0:96, :].bitcast(BF16)
        logits = part(qkT_flat, 448, 64).rearrange("p (t e) -> p t e", t=TT)
        top8 = part(qkT_flat, 512, 16).rearrange("p (t e) -> p t e", t=TT)
        idx8 = part(qkT_flat, 528, 16).rearrange("p (t e) -> p t e", t=TT)
        idxf = part(qkT_flat, 544, 16).rearrange("p (t e) -> p t e", t=TT)
        chosen = part(qkT_flat, 560, 64).rearrange("p (t e) -> p t e", t=TT)
        ex = part(qkT_flat, 624, 64).rearrange("p (t e) -> p t e", t=TT)
        wsum = part(qkT_flat, 688, 2)
        winv = part(qkT_flat, 690, 2)
        nmax2 = part(qkT_flat, 692, 2)
        rank = part(qkT_flat, 694, 66).rearrange("p (t e) -> p t e", t=TT)
        wgt = part(qkT_flat, 760, 64).rearrange("p (t e) -> p t e", t=TT)
        wT = part(qkT_flat, 824, 256)[0:32, :]
        cnt_row = part(qkT_flat, 1080, 32)[0:1, :]
        cnt_max = part(qkT_flat, 1112, 1)[0:1, :]
        cnt_int = part(qkT_flat, 1113, 1)[0:1, :].bitcast(I32)
        br_row = part(qkT_flat, 1114, 32)[0:1, :]
        ss2 = part(qkT_flat, 1146, 2)
        std2 = part(qkT_flat, 1148, 2)
        sq2 = part(qkT_flat, 1152, 1024)
        m_gate = part(gT_flat, 0, 1024)[0:CAP, :]
        m_sig = part(gT_flat, 1024, 1024)[0:CAP, :]
        m_up = part(gT_flat, 2048, 1024)[0:CAP, :]
        m_act = part(gT_flat, 3072, 1024)[0:CAP, :]

        wgu = a["w_gate_up"][0]
        wdn = a["w_down"][0]

        def slot(s):
            return ring[:, SLOT * s:SLOT * (s + 1)]

        def moe_weights(sp, e, s):
            if s < KT:
                src = wgu[bass.ds(e, 1), P * s:P * (s + 1), :].rearrange("o p n -> p (o n)")
                return sp.dma_start(slot(s), src)
            i = s - KT
            src = wdn[bass.ds(e, 1), 2 * P * i:2 * P * (i + 1), :].rearrange("o (k p) n -> p (o k) n", p=P)
            return sp.dma_start(slot(s).rearrange("p (k n) -> p k n", k=2), src)

        def table(eng, d, link):
            ks = slice(16 * d, 16 * d + 16)
            Ec, Es = E[:, 0, ks, :], E[:, 1, ks, :]
            t1, t2 = Etmp[:, d, 0], Etmp[:, d, 1]
            eng.memset(Ec[:, :, 0:1], 1.0)
            eng.memset(Es[:, :, 0:1], 0.0)
            eng.tensor_copy(Ec[:, :, 1:2], PAR[:, 1, ks].unsqueeze(2))
            link(eng.tensor_copy(Es[:, :, 1:2], PAR[:, 2, ks].unsqueeze(2)))
            for k in range(1, 8):
                lo, hi = 2 ** (k - 1), 2 ** k
                c, s = Ec[:, :, lo:lo + 1], Es[:, :, lo:lo + 1]
                if k < 7:
                    c2, s2 = Ec[:, :, hi:hi + 1], Es[:, :, hi:hi + 1]
                else:
                    c2, s2 = E128[:, 0, ks].unsqueeze(2), E128[:, 1, ks].unsqueeze(2)
                eng.tensor_tensor(t1[:, :, 0:1], c, c, ALU.mult)
                eng.tensor_tensor(t2[:, :, 0:1], s, s, ALU.mult)
                link(eng.tensor_tensor(t1[:, :, 1:2], c, s, ALU.mult))
                eng.tensor_tensor(c2, t1[:, :, 0:1], t2[:, :, 0:1], ALU.subtract)
                ins = eng.tensor_tensor(s2, t1[:, :, 1:2], t1[:, :, 1:2], ALU.add)
                if k == 7:
                    return ins
                link(ins)
                for j in range(1, hi, 32):
                    n = min(32, hi - j)
                    cj, sj = Ec[:, :, j:j + n], Es[:, :, j:j + n]
                    cb, sb = c2.to_broadcast([P, 16, n]), s2.to_broadcast([P, 16, n])
                    eng.tensor_tensor(t1[:, :, 0:n], cj, cb, ALU.mult)
                    link(eng.tensor_tensor(t2[:, :, 0:n], sj, sb, ALU.mult))
                    link(eng.tensor_tensor(Ec[:, :, hi + j:hi + j + n], t1[:, :, 0:n], t2[:, :, 0:n], ALU.subtract))
                    eng.tensor_tensor(t1[:, :, 0:n], cj, sb, ALU.mult)
                    link(eng.tensor_tensor(t2[:, :, 0:n], sj, cb, ALU.mult))
                    link(eng.tensor_tensor(Es[:, :, hi + j:hi + j + n], t1[:, :, 0:n], t2[:, :, 0:n], ALU.add))

        def frame(b):
            d, ks = tiles(b)
            dk = 16 * d + ks[0]
            return [E[:, r, dk:dk + 2, :].unsqueeze(2).to_broadcast([P, 2, 4, P]) for r in range(2)]

        def rotate_in(eng, b, link):
            s, (cos, sin) = b % 4, frame(b)
            eng.tensor_tensor(T4[s], X4[s], sin, ALU.mult)
            link(eng.tensor_tensor(X4[s], X4[s], cos, ALU.mult))
            eng.tensor_tensor(X[s][:, :, 0, :], X[s][:, :, 0, :], T[s][:, :, 1, :], ALU.add)
            return eng.tensor_tensor(X[s][:, :, 1, :], X[s][:, :, 1, :], T[s][:, :, 0, :], ALU.subtract)

        def rotate_out(eng, b):
            s, (cos, sin) = b % 4, frame(b)
            eng.tensor_tensor(T4[s], X4[s], sin, ALU.mult)
            return eng.tensor_tensor(X4[s], X4[s], cos, ALU.mult)

        block = ctx.enter_context(nc.Block())

        @block.sync
        def _(sp):
            x_rows = a["x"][0].rearrange("(t p) n -> p t n", p=P)
            for t in range(TT):
                sp.dma_start(xs[:, t, :], x_rows[:, t, :]).then_inc(S["x_in"], 16)
            for n, (src, _) in enumerate(units):
                if n >= PRO:
                    sp.wait_ge(*freed[n - PRO])
                sp.dma_start(unit(n), src).then_inc(slot_full[n % PRO], 16)
                if n == U_OUT:
                    sp.wait_ge(S["proj_done"], n_job)
                    sp.dma_start(x1[:, :, :], x_rows).then_inc(S["x_back"], 16)
            sp.wait_ge(S["zg_ready"], 1)
            for s in range(PRO, SLOTS):
                moe_weights(sp, 0, s).then_inc(slot_full[s], 16)
            for s in sorted(range(PRO), key=lambda s: max(range(s, n_units, PRO))):
                sp.wait_ge(*freed[max(range(s, n_units, PRO))])
                moe_weights(sp, 0, s).then_inc(slot_full[s], 16)
            with sp.Fori(1, EXPERTS) as e:
                for s in range(SLOTS):
                    sp.wait_ge(M["unit_used"], e * SLOTS + (s + 1 - SLOTS))
                    moe_weights(sp, e, s).then_inc(slot_full[s], 16)
            sp.wait_ge(S["passes_known"], 1)
            fullest = sp.value_load(cnt_int[0:1, 0:1], min_val=0, max_val=SEQ)
            with sp.Fori(1, PASSES) as p:
                with sp.If(fullest > p * CAP):
                    with sp.Fori(0, EXPERTS) as e:
                        for s in range(SLOTS):
                            sp.wait_ge(M["unit_used"], p * (EXPERTS * SLOTS) + e * SLOTS + (s + 1 - SLOTS))
                            moe_weights(sp, e, s).then_inc(slot_full[s], 16)
                    sp.nop()
                with sp.Else():
                    sp.nop()
                sp.nop()
            o_rows = out[0].rearrange("(t p) n -> p t n", p=P)
            for t in range(TT):
                sp.wait_ge(S["out_ready"], 2 * t + 2)
                sp.dma_start(o_rows[:, t, :], x1[:, t, :]).then_inc(S["out_stored"], 16)
            sp.wait_ge(S["out_stored"], 16 * TT)

        @block.scalar
        def _(act):
            copy = lambda o, i, **k: nc.scalar.activation(o, i, ACT.Copy, **k)

            for v_, name in ((0, "lam_re"), (1, "lam_im")):
                act.dma_start(PR[:, v_, :], a[name][0].rearrange("d (k g) s -> (d k) (g s)", g=2)).then_inc(S["lam_in"], 16)
            act.dma_start(ldt[0:32, 0:2], a["log_dt"][0].rearrange("d (k g) -> (d k) g", g=2)).then_inc(S["lam_in"], 16)
            act.dma_start(gain1, a["norm1"][0:1, :].to_broadcast([P, D])).then_inc(S["gain1_in"], 16)
            act.dma_start(ident[:, :], consts["ident"]).then_inc(S["ident_in"], 16)
            for r, name in ((0, "b_re"), (1, "b_im")):
                act.dma_start(Bn[:, r], a[name][0].rearrange("d g s c -> (d g s) c").rearrange("(k p) c -> p k c", p=P)).then_inc(S["bc_in"], 16)
            for r, name in ((0, "c_re"), (1, "c_im")):
                src = a[name][0].rearrange("d g c s -> (d g c) s").rearrange("(n p) s -> p n s", p=P)
                for u in range(2):
                    act.dma_start(Cn[:, r, :, u, :], src).then_inc(S["bc_in"], 16)
            act.dma_start(rope[:, :, :], consts["rope"]).then_inc(S["rope_in"], 16)
            act.dma_start(masks[:, :, :], consts["masks"]).then_inc(S["rope_in"], 16)
            act.dma_start(qk_gain[:, 0:VW], a["q_norm"].rearrange("o h d -> o (h d)").to_broadcast([P, VW])).then_inc(S["rope_in"], 16)
            act.dma_start(qk_gain[:, VW:QKW], a["k_norm"].rearrange("o h d -> o (h d)").to_broadcast([P, VW])).then_inc(S["rope_in"], 16)
            with nc.allow_non_contiguous_dma("one column of 512 values"):
                act.dma_start(d_col[:, :], a["d_skip"][0].rearrange("(m g) c -> (g c) m", m=4)).then_inc(S["cols_in"], 16)
                act.dma_start(bglu_col[:, :], a["b_glu"][0].rearrange("(m p) -> p m", p=P)).then_inc(S["cols_in"], 16)

            act.wait_ge(S["lam_in"], 48)
            nc.scalar.activation(dt_row[0:32, :], ldt[0:32, 0:2], ACT.Exp).then_inc(S["dt_ready"], 1)
            act.wait_ge(S["rows_ready"], 1)
            nc.scalar.activation(PR[:, 4, :], PR[:, 3, :], ACT.Exp).then_inc(S["mag_ready"], 1)
            for t in range(TT):
                act.wait_ge(S["x_in"], 16 * TT)
                if t:
                    act.wait_ge(S["sq_done"], t)
                nc.scalar.activation(square[:, :], xs[:, t, :], ACT.Square, accum_out=ss[:, t:t + 1]).then_inc(S["sq_done"], 1)
            act.wait_ge(S["std_done"], 1)
            nc.scalar.activation(rstd[:, :], rstd[:, :], ACT.Sqrt).then_inc(S["std_done"], 1)
            act.wait_ge(S["rows_ready"], 2)
            nc.scalar.activation(PR[:, 5, :], PR[:, 2, :], ACT.Sin)
            nc.scalar.activation(PR[:, 6, :], PR[:, 2, :], ACT.Sin, scale=0.5).then_inc(S["sin_ready"], 1)
            for b in (0, 2):
                act.wait_ge(S["hT_trans"], b + 1)
                copy(hT[:, 2 * b:2 * b + 2, :], banks[b][:, :]).then_inc(S["hT_copy"], 1)
            for i in range(2):
                act.wait_ge(S["uT_done"], i + 1)
                src = banks[4 + i][:, :].rearrange("p (m t) -> p m t", m=2)
                copy(uT[:, 2 * i:2 * i + 2, :], src)
                copy(uTr[:, 2 * i:2 * i + 2, ::-1], src).then_inc(S["uT_copy"], 1)
            for n in range(4):
                act.wait_ge(S["bd_trans"], n + 1)
                copy(BT[:, 4 * n:4 * n + 4, :], banks[n][:, :]).then_inc(S["bd_copy"], 1)

            for step in steps:
                kind, i = step[0], step[1]
                if kind == "bu":
                    for k in range(2):
                        n = 2 * i + k
                        act.wait_ge(S["bu_done"], n + 1)
                        if i < 4 and k == 0:
                            act.wait_ge(S["table_fwd"], 1)
                            act.wait_ge(S["table_bwd"], 1)
                            act.wait_ge(S["c_trans"], 4)
                        if i >= 4 and k == 0:
                            act.wait_ge(S["ssm_y"], i - 3)
                        copy(X[i % 4][:, k].rearrange("p r t -> p (r t)"), banks[n % 2][:, :]).then_inc(S["bu_copied"], 1)
                elif kind == "qkv":
                    c, t = step[1], step[2]
                    j = JOB_QKV[c, t]
                    act.wait_ge(S["proj_done"], j + 1)
                    bank = banks[4 + j % 2]
                    if c < 3:
                        copy(raw[:, t, 512 * c:512 * c + 512], bank[:, :]).then_inc(S["proj_copied"], 1)
                    else:
                        w = 512 if c == 3 else 256
                        copy(v[:, t, 512 * (c - 3):512 * (c - 3) + w], bank[:, 0:w]).then_inc(S["proj_copied"], 1)
                elif kind == "qk_std":
                    act.wait_ge(S["qk_ms"], i + 1)
                    nc.scalar.activation(rs_qk[:, :], rs_qk[:, :], ACT.Sqrt).then_inc(S["qk_std"], 1)
                elif kind == "qkT":
                    t = i
                    for g in range(3):
                        act.wait_ge(S["qkT_done"], 3 * t + g + 1)
                        copy(qkT[:, 4 * g:4 * g + 4, P * t:P * t + P], banks[6 + (3 * t + g) % 2][:, :]).then_inc(S["qkT_copied"], 1)
                elif kind == "gate":
                    j = JOB_GATE[i]
                    act.wait_ge(S["proj_done"], j + 1)
                    if i == 0:
                        act.wait_ge(S["par_ready"], 1)
                    copy(gT[:, 2 * i:2 * i + 2, :], banks[4 + j % 2][:, :]).then_inc(S["proj_copied"], 1)
                elif kind == "scores":
                    act.wait_ge(S["pmax_ready"], i + 1)
                    pr = probs[:, i % 2, :]
                    nc.scalar.activation(pr, pr, ACT.Exp, bias=nmax[:, i:i + 1], accum_out=rsum[:, i:i + 1]).then_inc(S["exp_done"], 1)
                elif kind == "pt":
                    t = i % 2
                    act.wait_ge(S["pt_done"], i + 1)
                    if t == 0 and i >= 2:
                        act.wait_ge(S["proj_done"], JOB_PV[i // 2 - 1] + 1)
                    copy(probsT[:, 0:4, P * t:P * t + P], banks[6][:, :])
                    copy(probsT[:, 4:6, P * t:P * t + P], banks[7][:, 0:256]).then_inc(S["pt_copied"], 1)
                elif kind == "pv":
                    j = JOB_PV[i]
                    act.wait_ge(S["proj_done"], j + 1)
                    lo = HD * (i % 2)
                    copy(atT[lo:lo + HD, i // 2, :], banks[4 + j % 2][lo:lo + HD, 0:SEQ]).then_inc(S["proj_copied"], 1)
                elif kind == "y" and i == 7:
                    act.wait_ge(S["ssm_y"], 8)
                    for n in range(2):
                        ins = copy(yT[:, 2 * n:2 * n + 2, :], banks[2 + n][:, :])
                    ins.then_inc(S["yf_copied"], 1)

            act.wait_ge(S["proj_done"], n_job)
            act.wait_ge(S["ssm_y"], NB)
            for r in range(3):
                act.dma_start(bgu[32 * r:32 * r + 32, :], a["b_gate_up"][0]).then_inc(S["bias_in"], 16)
            for dst, src in ((pick, consts["pick"]), (bdn, a["b_down"][0]),
                             (wr[:, :, :], a["w_router"][0].rearrange("(k p) e -> p k e", p=P)),
                             (tri, consts["tri"]), (gain2, a["norm2"][0:1, :].to_broadcast([P, D])),
                             (iota2, consts["iota"]), (iota32, consts["iota32"]),
                             (br_row, a["b_router"][0:1, :])):
                act.dma_start(dst, src).then_inc(S["moe_in"], 16)

            act.wait_ge(S["yb_ready"], 1)
            nc.scalar.activation(z_th.rearrange("p m t -> p (m t)"), z_tmp.rearrange("p m t -> p (m t)"), ACT.Tanh, scale=GELU_C).then_inc(S["tanh_ready"], 1)
            act.wait_ge(S["proj_copied"], n_job)
            nc.scalar.activation(gT_flat, gT_flat, ACT.Sigmoid).then_inc(S["gates_ready"], 1)
            act.wait_ge(S["cols_in"], 32)
            for m in range(4):
                act.wait_ge(S["glu_done"], m // 2 + 1)
                nc.scalar.activation(z_sig[:, m, :], banks[4 + m // 2][:, SEQ * (m % 2):SEQ * (m % 2) + SEQ], ACT.Sigmoid,
                                     bias=bglu_col[:, m:m + 1]).then_inc(S["sig_ready"], 1)

            for t in range(TT):
                act.wait_ge(S["x1_ready"], 2 * t + 2)
                if t:
                    act.wait_ge(S["moe_sq"], t)
                nc.scalar.activation(sq2, x1[:, t, :], ACT.Square, accum_out=ss2[:, t:t + 1]).then_inc(S["moe_sq"], 1)
            act.wait_ge(S["moe_std"], 1)
            nc.scalar.activation(std2, std2, ACT.Sqrt).then_inc(S["moe_std"], 1)
            for b in (0, 2):
                act.wait_ge(S["h2T_done"], b + 1)
                copy(h2T[:, 2 * b:2 * b + 2, :], banks[b][:, :]).then_inc(S["h2T_copied"], 1)
            act.wait_ge(S["negmax_ready"], 1)
            for t in range(TT):
                ins = nc.scalar.activation(ex[:, t, :], logits[:, t, :], ACT.Exp, bias=nmax2[:, t:t + 1])
            ins.then_inc(S["ex_ready"], 1)
            act.wait_ge(S["wt_done"], 1)
            copy(wT, banks[5][0:32, 0:256]).then_inc(S["wt_copied"], 1)

            def first_rows(p):
                act.wait_ge(M["gathered"], p * 33 + 1)
                copy(XeT.rearrange("p k r -> p (k r)"), banks[6][:, :]).then_inc(M["xT"], 1)
                act.wait_ge(M["y_low"], p * 33 + 1)
                copy(ysb[0:1, 512:513], ysb[0:1, 512:513]).then_inc(M["y_high"], 1)

            def expert(p, i, b):
                n = p * EXPERTS + i * 2 + b
                for ch in range(2):
                    act.wait_ge(M["gmin"], 2 * n + ch + 1)
                    sl = slice(512 * ch, 512 * ch + 512)
                    nc.scalar.activation(m_sig[:, sl], m_gate[:, sl], ACT.Sigmoid, scale=1.702).then_inc(M["sigm"], 1)
                act.wait_ge(M["gathered"], p * 33 + i * 2 + b + 2)
                copy(XeT.rearrange("p k r -> p (k r)"), banks[6][:, :]).then_inc(M["xT"], 1)
                if b == 0:
                    act.wait_ge(M["swt"], p * PAIRS + i + 1)
                    copy(SW, banks[7][:, 0:SEQ]).then_inc(M["scatter_w"], 1)
                act.wait_ge(M["act_trans"], n + 1)
                copy(acT.rearrange("p k r -> p (k r)"), banks[6][:, :]).then_inc(M["actT"], 1)
                act.wait_ge(M["unit_used"], (n + 1) * SLOTS)
                copy(ysb[CAP * b:CAP * b + CAP, 512:1024], banks[7][CAP:2 * CAP, :]).then_inc(M["y_high"], 1)

            first_rows(0)
            with act.Fori(0, PAIRS) as i:
                expert(0, i, 0)
                expert(0, i, 1)
            act.wait_ge(S["passes_known"], 1)
            fullest = act.value_load(cnt_int[0:1, 0:1], min_val=0, max_val=SEQ)
            with act.Fori(1, PASSES) as p:
                with act.If(fullest > p * CAP):
                    first_rows(p)
                    with act.Fori(0, PAIRS) as i:
                        expert(p, i, 0)
                        expert(p, i, 1)
                    act.nop()
                with act.Else():
                    act.nop()
                act.nop()

        @block.vector
        def _(dve):
            chain = [0]
            V = nc.vector

            def link(ins):
                chain[0] += 1
                ins.then_inc(S["dve_chain"], 1)
                dve.wait_ge(S["dve_chain"], chain[0])

            row = lambda n: PR[:, n, :]
            LR, LI, ANG, LRDT, MAG, SIN, HSIN = (row(n) for n in range(7))
            COS, ABR, ABI, DEN, FR, FI, T1, T2, K_ = (row(n) for n in range(7, 16))
            dt_b = dt_row[0:32, :].unsqueeze(2).to_broadcast([32, 2, HD])
            by_group = lambda r: r.rearrange("p (g s) -> p g s", g=2)

            link(V.memset(XT_flat[:, 2048:4096], 0.0))
            link(V.memset(CT_flat, 0.0))
            dve.wait_ge(S["dt_ready"], 1)
            V.tensor_tensor(by_group(LRDT), by_group(LR), dt_b, ALU.mult).then_inc(S["rows_ready"], 1)
            link(V.tensor_tensor(by_group(ANG), by_group(LI), dt_b, ALU.mult))
            link(V.tensor_scalar(K_, ANG, INV_2PI, ROUND, ALU.mult, ALU.add))
            link(V.tensor_scalar(K_, K_, -ROUND, None, ALU.add))
            for piece in (PI_1, PI_2, PI_3):
                link(V.scalar_tensor_tensor(out=ANG, in0=K_, scalar=-piece, in1=ANG, op0=ALU.mult, op1=ALU.add))
            V.tensor_scalar(ANG, ANG, 3.1415925, -3.1415925, ALU.min, ALU.max).then_inc(S["rows_ready"], 1)
            dve.wait_ge(S["sq_done"], TT)
            V.tensor_scalar(rstd[:, :], ss[:, :], 1.0 / D, EPS, ALU.mult, ALU.add).then_inc(S["std_done"], 1)
            dve.wait_ge(S["std_done"], 2)
            link(V.reciprocal(rstd[:, :], rstd[:, :]))
            dve.wait_ge(S["gain1_in"], 16)
            for t in range(TT):
                V.scalar_tensor_tensor(out=xs[:, t, :], in0=xs[:, t, :], scalar=rstd[:, t:t + 1], in1=gain1,
                                       op0=ALU.mult, op1=ALU.mult).then_inc(S["h_ready"], 1)
            dve.wait_ge(S["sin_ready"], 1)
            link(V.tensor_tensor(COS, HSIN, HSIN, ALU.mult))
            link(V.tensor_scalar(COS, COS, -2.0, 1.0, ALU.mult, ALU.add))
            dve.wait_ge(S["mag_ready"], 1)
            V.tensor_tensor(ABR, MAG, COS, ALU.mult)
            V.tensor_tensor(ABI, MAG, SIN, ALU.mult)
            V.tensor_tensor(T1, LR, LR, ALU.mult)
            link(V.tensor_tensor(T2, LI, LI, ALU.mult))
            V.tensor_scalar(ABR, ABR, -1.0, None, ALU.add)
            link(V.tensor_tensor(DEN, T1, T2, ALU.add))
            V.reciprocal(DEN, DEN)
            V.tensor_tensor(T1, ABR, LR, ALU.mult)
            link(V.tensor_tensor(T2, ABI, LI, ALU.mult))
            link(V.tensor_tensor(FR, T1, T2, ALU.add))
            V.tensor_tensor(T1, ABI, LR, ALU.mult)
            link(V.tensor_tensor(T2, ABR, LI, ALU.mult))
            link(V.tensor_tensor(FI, T1, T2, ALU.subtract))
            V.tensor_tensor(FR, FR, DEN, ALU.mult)
            V.tensor_tensor(FI, FI, DEN, ALU.mult).then_inc(S["rows_ready"], 1)
            for b in (1, 3):
                dve.wait_ge(S["hT_trans"], b + 1)
                V.tensor_copy(hT[:, 2 * b:2 * b + 2, :], banks[b][:, :].rearrange("p (k t) -> p k t", k=2)).then_inc(S["hT_copy"], 1)
            dve.wait_ge(S["par_trans"], 1)
            V.tensor_copy(PAR[:, :, :], banks[6][:, 0:160].rearrange("p (v k) -> p v k", v=5)).then_inc(S["par_ready"], 1)
            dve.wait_ge(S["par_ready"], 1)
            dve.wait_ge(S["bc_in"], 96)
            f_re = PAR[:, 3, :].unsqueeze(2).to_broadcast([P, 32, 16])
            f_im = PAR[:, 4, :].unsqueeze(2).to_broadcast([P, 32, 16])
            for r, (p0, p1, op) in enumerate(((f_re, f_im, ALU.subtract), (f_im, f_re, ALU.add))):
                V.tensor_tensor(Btmp[:, 0], Bn[:, 0], p0, ALU.mult)
                link(V.tensor_tensor(Btmp[:, 1], Bn[:, 1], p1, ALU.mult))
                for g in range(2):
                    h = slice(HD * g, HD * g + HD)
                    ins = V.tensor_tensor(BD[h, r, :, g, :], Btmp[h, 0], Btmp[h, 1], op)
                if r == 0:
                    link(ins)
                else:
                    ins.then_inc(S["bd_ready"], 1)
            for n in range(4):
                d, r = n % 2, n // 2
                dve.wait_ge(S["c_trans"], n + 1)
                src = banks[4 + n][:, :].rearrange("p (k g c) -> p k g c", k=16, g=2)
                for vv, sign in (((0, 1.0), (1, -1.0)) if r == 0 else ((2, -1.0),)):
                    for g in range(2):
                        h = slice(HD * g, HD * g + HD)
                        ins = V.tensor_scalar(CT[h, d, vv, :, g, :], src[h, :, g, :], sign, None, ALU.mult)
                ins.then_inc(S["c_copy"], 1)

            table(V, 0, link).then_inc(S["table_fwd"], 1)

            def scan(b):
                s, (d, ks) = b % 4, tiles(b)
                dk = 16 * d + ks[0]
                cr, g1, g2 = (part(carry, 4 * n, 4).rearrange("p (k r) -> p k r", k=2) for n in range(3))
                for half in range(2):
                    for k in range(2):
                        mag = PAR[:, 0, dk + k:dk + k + 1].to_broadcast([P, P])
                        for r in range(2):
                            seg = X[s][:, k, r, P * half:P * half + P]
                            ins = V.tensor_tensor_scan(seg, mag, seg, cr[:, k, r:r + 1] if half else 0.0, ALU.mult, ALU.add)
                    if half == 0:
                        link(ins)
                        last = X[s][:, :, :, P - 1]
                        V.tensor_tensor(g1, last, E128[:, 0, dk:dk + 2].unsqueeze(2).to_broadcast([P, 2, 2]), ALU.mult)
                        link(V.tensor_tensor(g2, last, E128[:, 1, dk:dk + 2].unsqueeze(2).to_broadcast([P, 2, 2]), ALU.mult))
                        V.tensor_tensor(cr[:, :, 0], g1[:, :, 0], g2[:, :, 1], ALU.subtract)
                        link(V.tensor_tensor(cr[:, :, 1], g1[:, :, 1], g2[:, :, 0], ALU.add))
                ins.then_inc(S["scan_done"], 1)

            def qk_norm(t):
                dve.wait_ge(S["proj_copied"], JOB_QKV[2, t] + 1)
                if t == 0:
                    dve.wait_ge(S["rope_in"], 64)
                else:
                    dve.wait_ge(S["qk_ready"], t)
                tmp = qkT_flat[:, 0:QKW]
                t3 = tmp.rearrange("p (h d) -> p h d", h=NQK)
                link(V.tensor_tensor(tmp, raw[:, t, :], raw[:, t, :], ALU.mult))
                link(V.tensor_reduce(ss_qk[:, :], t3, AXX, ALU.add))
                V.tensor_scalar(rs_qk[:, :], ss_qk[:, :], 1.0 / HD, EPS, ALU.mult, ALU.add).then_inc(S["qk_ms"], 1)

            def qk_rotate(t):
                r3 = raw[:, t, :].rearrange("p (h d) -> p h d", h=NQK)
                t3 = qkT_flat[:, 0:QKW].rearrange("p (h d) -> p h d", h=NQK)
                t4 = qkT_flat[:, QKW:2 * QKW].rearrange("p (h d) -> p h d", h=NQK)
                dve.wait_ge(S["qk_std"], t + 1)
                link(V.reciprocal(rs_qk[:, :], rs_qk[:, :]))
                link(V.tensor_tensor(r3, r3, rs_qk[:, :].unsqueeze(2).to_broadcast([P, NQK, HD]), ALU.mult))
                link(V.tensor_tensor(raw[:, t, :], raw[:, t, :], qk_gain[:, :], ALU.mult))
                cos = rope[:, t, 0:32].unsqueeze(1).to_broadcast([P, NQK, 32])
                sin = rope[:, t, 32:64].unsqueeze(1).to_broadcast([P, NQK, 32])
                a1, a2 = r3[:, :, 0:32], r3[:, :, 32:64]
                V.tensor_tensor(t3[:, :, 0:32], a1, cos, ALU.mult)
                V.tensor_tensor(t3[:, :, 32:64], a2, cos, ALU.mult)
                V.tensor_tensor(t4[:, :, 0:32], a2, sin, ALU.mult)
                link(V.tensor_tensor(t4[:, :, 32:64], a1, sin, ALU.mult))
                V.tensor_tensor(a1, t3[:, :, 0:32], t4[:, :, 0:32], ALU.subtract)
                V.tensor_tensor(a2, t3[:, :, 32:64], t4[:, :, 32:64], ALU.add).then_inc(S["qk_ready"], 1)

            def softmax(i):
                t = i % 2
                pr = probs[:, i % 2, :]
                dve.wait_ge(S["scores_done"], i + 1)
                if i == 0:
                    dve.wait_ge(S["qkT_done"], 6)
                V.scalar_tensor_tensor(out=pr[:, 0:512], in0=banks[6][:, :], scalar=HD ** -0.5, in1=masks[:, t, 0:512],
                                       op0=ALU.mult, op1=ALU.add)
                link(V.scalar_tensor_tensor(out=pr[:, 512:VW], in0=banks[7][:, 0:256], scalar=HD ** -0.5,
                                            in1=masks[:, t, 512:VW], op0=ALU.mult, op1=ALU.add))
                link(V.reduce_max(rinv[:, i:i + 1], pr, AXX))
                V.tensor_scalar(nmax[:, i:i + 1], rinv[:, i:i + 1], -1.0, None, ALU.mult).then_inc(S["pmax_ready"], 1)
                dve.wait_ge(S["exp_done"], i + 1)
                link(V.reciprocal(rinv[:, i:i + 1], rsum[:, i:i + 1]))
                V.tensor_scalar(pr, pr, rinv[:, i:i + 1], None, ALU.mult).then_inc(S["probs_ready"], 1)

            def pair(n):
                b = 2 * n
                dve.wait_ge(S["bu_copied"], 2 * b + 2)
                link(rotate_in(V, b, link))
                scan(b)
                dve.wait_ge(S["scan_done"], b + 1)
                rotate_out(V, b).then_inc(S["rout_even"], 1)
                dve.wait_ge(S["rin_odd"], n + 1)
                scan(b + 1)

            dve.wait_ge(S["table_fwd"], 1)
            pair(0)
            pair(1)
            qk_norm(0)
            pair(2)
            qk_rotate(0)
            qk_norm(1)
            pair(3)
            qk_rotate(1)
            dve.wait_ge(S["table_bwd"], 1)
            pair(4)
            softmax(0)
            softmax(1)
            pair(5)
            softmax(2)
            softmax(3)
            pair(6)
            softmax(4)
            softmax(5)
            pair(7)
            softmax(6)
            softmax(7)

            dve.wait_ge(S["cols_in"], 32)
            dve.wait_ge(S["ssm_y"], NB)
            dve.wait_ge(S["yf_copied"], 1)
            for n in range(2):
                back = banks[2 + n][:, :].rearrange("p (m t) -> p m t", m=2)[:, :, ::-1]
                ins = V.tensor_tensor(yT[:, 2 * n:2 * n + 2, :], yT[:, 2 * n:2 * n + 2, :], back, ALU.add)
            link(ins)
            for m in range(4):
                ins = V.scalar_tensor_tensor(out=yT[:, m, :], in0=uT[:, m, :], scalar=d_col[:, m:m + 1], in1=yT[:, m, :],
                                             op0=ALU.mult, op1=ALU.add)
            link(ins)
            link(V.tensor_tensor(z_tmp, yT, yT, ALU.mult))
            link(V.tensor_scalar(z_tmp, z_tmp, GELU_A, 1.0, ALU.mult, ALU.add))
            V.tensor_tensor(z_tmp, z_tmp, yT, ALU.mult).then_inc(S["yb_ready"], 1)
            dve.wait_ge(S["tanh_ready"], 1)
            link(V.tensor_scalar(z_th, z_th, 1.0, 0.5, ALU.add, ALU.mult))
            V.tensor_tensor(z, z_th, yT, ALU.mult).then_inc(S["z_ready"], 1)
            dve.wait_ge(S["z_ready"], 1)
            dve.wait_ge(S["sig_ready"], 4)
            V.tensor_tensor(zg, z, z_sig, ALU.mult).then_inc(S["zg_ready"], 1)
            dve.wait_ge(S["gates_ready"], 1)
            for n in range(4):
                dve.wait_ge(S["ya_done"], n + 1)
                g0 = gT[:, 2 * n:2 * n + 2, :]
                ins = V.tensor_tensor(g0, g0, banks[YA_BANK[n]][:, :].rearrange("p (m t) -> p m t", m=2), ALU.mult)
            link(ins)
            for n in range(4):
                dve.wait_ge(S["ys_done"], n + 1)
                g1 = gT[:, 8 + 2 * n:10 + 2 * n, :]
                link(V.tensor_tensor(g1, g1, banks[YS_BANK[n]][:, :].rearrange("p (m t) -> p m t", m=2), ALU.mult))
                V.tensor_tensor(mT[:, 2 * n:2 * n + 2, :], gT[:, 2 * n:2 * n + 2, :], g1, ALU.add).then_inc(S["mixed_ready"], 1)
            dve.wait_ge(S["x_back"], 16)
            for n in range(4):
                t, ch = n // 2, n % 2
                dve.wait_ge(S["xo_done"], n + 1)
                o = x1[:, t, 512 * ch:512 * ch + 512]
                V.tensor_tensor(o, o, banks[XO_BANK[n]][:, :], ALU.add).then_inc(S["x1_ready"], 1)

            dve.wait_ge(S["moe_in"], 16 * 8)
            dve.wait_ge(S["moe_sq"], TT)
            V.tensor_scalar(std2, ss2, 1.0 / D, EPS, ALU.mult, ALU.add).then_inc(S["moe_std"], 1)
            V.memset(ones, 1.0)
            V.memset(ysb, 0.0)
            V.memset(SW, 0.0)
            V.memset(rank[:, :, 32:33], BIG).then_inc(M["y_low"], 1)
            dve.wait_ge(S["moe_std"], 2)
            link(V.reciprocal(std2, std2))
            for t in range(TT):
                V.scalar_tensor_tensor(out=h2[:, t, :], in0=x1[:, t, :], scalar=std2[:, t:t + 1], in1=gain2,
                                       op0=ALU.mult, op1=ALU.mult).then_inc(S["h2_ready"], 1)
            for b in (1, 3):
                dve.wait_ge(S["h2T_done"], b + 1)
                V.tensor_copy(h2T[:, 2 * b:2 * b + 2, :], banks[b][:, :].rearrange("p (k t) -> p k t", k=2)).then_inc(S["h2T_copied"], 1)
            dve.wait_ge(S["logit_done"], 1)
            link(V.tensor_copy(logits, banks[4][:, 0:64].rearrange("p (t e) -> p t e", t=TT)))
            for t in range(TT):
                link(V.max(top8[:, t, :], logits[:, t, :]))
                link(V.max_index(idx8[:, t, :].bitcast(U32), top8[:, t, :], logits[:, t, :]))
            V.tensor_scalar(nmax2, top8[:, :, 0], -1.0, None, ALU.mult).then_inc(S["negmax_ready"], 1)
            link(V.tensor_copy(idxf, idx8.bitcast(U32)))
            for t in range(TT):
                link(V.tensor_scalar(chosen[:, t, :], iota32, idxf[:, t, 0:1], None, ALU.is_equal))
                for j in range(1, 4):
                    ins = V.scalar_tensor_tensor(out=chosen[:, t, :], in0=iota32, scalar=idxf[:, t, j:j + 1],
                                                 in1=chosen[:, t, :], op0=ALU.is_equal, op1=ALU.add)
                    if (t, j) != (TT - 1, 3):
                        link(ins)
            ins.then_inc(S["route_ready"], 1)
            dve.wait_ge(S["route_ready"], 1)
            dve.wait_ge(S["ex_ready"], 1)
            link(V.tensor_tensor(wgt, ex, chosen, ALU.mult))
            link(V.tensor_reduce(wsum, wgt, AXX, ALU.add))
            link(V.reciprocal(winv, wsum))
            V.tensor_tensor(wgt, wgt, winv.unsqueeze(2).to_broadcast([P, TT, 32]), ALU.mult).then_inc(S["route_ready"], 1)
            dve.wait_ge(S["route_ready"], 2)
            dve.wait_ge(S["rank_done"], 1)
            link(V.tensor_scalar(chosen, chosen, -BIG, BIG, ALU.mult, ALU.add))
            link(V.tensor_tensor(rank[:, :, 0:32], chosen, banks[4][:, 64:128].rearrange("p (t e) -> p t e", t=TT), ALU.add))
            V.tensor_copy(cnt_row, banks[4][0:1, 128:160]).then_inc(S["counted"], 1)
            dve.wait_ge(S["counted"], 1)
            link(V.reduce_max(cnt_max, cnt_row, AXX))
            V.tensor_copy(cnt_int, cnt_max).then_inc(S["passes_known"], 1)

            def onehots(p, e):
                for t in range(TT):
                    ins = V.tensor_scalar(G[:, t, :], iota2, rank[:, t, bass.ds(e, 1)], None, ALU.is_equal)
                return ins

            def expert(p, i, b):
                n, e = p * EXPERTS + i * 2 + b, i * 2 + b

                def half(ch):
                    sl, m = slice(512 * ch, 512 * ch + 512), 2 * n + ch + 1
                    V.tensor_scalar(m_gate[:, sl], banks[4 + ch][0:CAP, :], 7.0, None, ALU.min).then_inc(M["gmin"], 1)
                    V.tensor_scalar(m_up[:, sl], banks[4 + ch][CAP:2 * CAP, :], 7.0, -7.0, ALU.min, ALU.max).then_inc(M["clipped"], 1)
                    dve.wait_ge(M["clipped"], m)
                    V.scalar_tensor_tensor(out=m_up[:, sl], in0=m_up[:, sl], scalar=1.0, in1=m_gate[:, sl],
                                           op0=ALU.add, op1=ALU.mult).then_inc(M["up_gate"], 1)
                    dve.wait_ge(M["up_gate"], m)
                    dve.wait_ge(M["sigm"], m)
                    V.tensor_tensor(m_act[:, sl], m_up[:, sl], m_sig[:, sl], ALU.mult).then_inc(M["act_ready"], 1)

                if b == 0:
                    for t in range(TT):
                        for u in range(2):
                            ins = V.tensor_scalar(GW[:, t, u, :], iota2, rank[:, t, bass.ds(e + u, 1)], wgt[:, t, bass.ds(e + u, 1)],
                                                  ALU.is_equal, ALU.mult)
                    ins.then_inc(M["gw_ready"], 1)
                dve.wait_ge(M["half_done"], n + 1)
                half(0)
                onehots(p, e + 1)
                V.tensor_copy(sel, pick[:, bass.ds(e + 1, 1)].to_broadcast([96, CAP])).then_inc(M["onehots"], 1)
                dve.wait_ge(M["unit_used"], n * SLOTS + KT)
                half(1)
                dve.wait_ge(M["unit_used"], (n + 1) * SLOTS)
                V.tensor_copy(ysb[CAP * b:CAP * b + CAP, 0:512], banks[7][0:CAP, :]).then_inc(M["y_low"], 1)

            def start_pass(p):
                V.tensor_copy(sel, pick[:, 0:1].to_broadcast([96, CAP]))
                onehots(p, 0).then_inc(M["onehots"], 1)

            start_pass(0)
            with dve.Fori(0, PAIRS) as i:
                expert(0, i, 0)
                expert(0, i, 1)
            fullest = dve.value_load(cnt_int[0:1, 0:1], min_val=0, max_val=SEQ)
            with dve.Fori(1, PASSES) as p:
                with dve.If(fullest > p * CAP):
                    dve.wait_ge(S["acc_done"], p)
                    V.tensor_scalar(iota2, iota2, float(CAP), None, ALU.add).then_inc(M["iota_ready"], 1)
                    dve.wait_ge(M["iota_ready"], p)
                    V.memset(ysb, 0.0).then_inc(M["y_low"], 1)
                    start_pass(p)
                    with dve.Fori(0, PAIRS) as i:
                        expert(p, i, 0)
                        expert(p, i, 1)
                    dve.nop()
                with dve.Else():
                    dve.nop()
                dve.nop()
            dve.wait_ge(S["acc_done"], PASSES)
            for n in range(4):
                t, ch = n // 2, n % 2
                o = x1[:, t, 512 * ch:512 * ch + 512]
                V.tensor_tensor(o, o, banks[n][:, :], ALU.add).then_inc(S["out_ready"], 1)

        @block.gpsimd
        def _(pool):
            chain = [0]

            def link(ins):
                chain[0] += 1
                ins.then_inc(S["pool_chain"], 1)
                pool.wait_ge(S["pool_chain"], chain[0])

            pool.wait_ge(S["par_ready"], 1)
            table(nc.gpsimd, 1, link).then_inc(S["table_bwd"], 1)
            pool.wait_ge(S["table_bwd"], 1)
            pool.wait_ge(S["table_fwd"], 1)
            odd = list(range(1, NB, 2))
            for n in range(len(odd) + 1):
                if n < len(odd):
                    pool.wait_ge(S["bu_copied"], 2 * odd[n] + 2)
                    rotate_in(nc.gpsimd, odd[n], link).then_inc(S["rin_odd"], 1)
                if n >= 1:
                    pool.wait_ge(S["scan_done"], odd[n - 1] + 1)
                    rotate_out(nc.gpsimd, odd[n - 1]).then_inc(S["rout_odd"], 1)
            pool.wait_ge(S["bias_in"], 48)
            link(nc.gpsimd.tensor_copy(bgu3[0:32, :], bgu[0:32, :]))
            link(nc.gpsimd.tensor_copy(bgu_t, bgu))
            link(nc.gpsimd.tensor_tensor(bgu, bgu, bgu_t, ALU.subtract))
            link(nc.gpsimd.tensor_copy(bgu3[32:64, :], bgu[32:64, :]))
            link(nc.gpsimd.tensor_copy(bgu_t, bgu))
            link(nc.gpsimd.tensor_tensor(bgu, bgu, bgu_t, ALU.subtract))
            nc.gpsimd.tensor_copy(bgu3[64:96, :], bgu[64:96, :]).then_inc(S["bias_parts"], 1)

        @block.tensor
        def _(pe):
            mm, transpose = nc.tensor.matmul, nc.tensor.transpose
            pe.wait_ge(S["ident_in"], 16)
            pe.wait_ge(S["h_ready"], TT)
            for b in range(4):
                for kk in range(2):
                    for t in range(TT):
                        ins = transpose(banks[b][:, P * (2 * kk + t):P * (2 * kk + t + 1)],
                                        xs[:, t, P * (2 * b + kk):P * (2 * b + kk + 1)], ident[:, :])
                ins.then_inc(S["hT_trans"], 1)
            pe.wait_ge(S["rows_ready"], 3)
            for n, r in enumerate((4, 7, 5, 11, 12)):
                ins = transpose(banks[6][:, 32 * n:32 * n + 32], PR[:, r, :], ident[0:32, 0:32])
            ins.then_inc(S["par_trans"], 1)
            pe.wait_ge(S["hT_copy"], 4)
            for s in range(2):
                pe.wait_ge(slot_full[s], 16)
            for m in range(4):
                for kt in range(KT):
                    ins = mm(banks[4 + m // 2][:, SEQ * (m % 2):SEQ * (m % 2) + SEQ],
                             unit(kt // 4)[:, kt % 4, P * m:P * m + P], hT[:, kt, :], start=kt == 0, stop=kt == KT - 1)
                if m % 2:
                    ins.then_inc(S["uT_done"], 1)
            pe.wait_ge(S["bd_ready"], 1)
            for n in range(4):
                for j in range(4):
                    ins = transpose(banks[n][:, P * j:P * j + P], BDt[:, 4 * n + j, :], ident[:, :])
                ins.then_inc(S["bd_trans"], 1)
            pe.wait_ge(S["uT_copy"], 2)
            pe.wait_ge(S["par_ready"], 1)
            for n in range(4):
                for j in range(4):
                    ins = transpose(banks[4 + n][:, P * j:P * j + P], Cn_t[:, 4 * n + j, :], ident[:, :])
                ins.then_inc(S["c_trans"], 1)

            def job_bank(j):
                if j < 2:
                    pe.wait_ge(S["c_copy"], 4)
                else:
                    pe.wait_ge(S["proj_copied"], j - 1)
                return banks[4 + j % 2]

            def loaded(n):
                pe.wait_ge(slot_full[n % PRO], 16 * (n // PRO + 1))

            for step in steps:
                kind, i = step[0], step[1]
                if kind == "bu":
                    d, ks = tiles(i)
                    if i == 0:
                        pe.wait_ge(S["bd_copy"], 4)
                    for k, kk in enumerate(ks):
                        n = 2 * i + k
                        if n >= 2:
                            pe.wait_ge(S["bu_copied"], n - 1)
                        m, q = kk // 4, slice(32 * (kk % 4), 32 * (kk % 4) + 32)
                        for r in range(2):
                            ins = mm(banks[n % 2][:, SEQ * r:SEQ * r + SEQ], BT[q, 8 * r + 4 * d + m, :],
                                     (uTr if d else uT)[q, m, :], start=True, stop=True)
                        ins.then_inc(S["bu_done"], 1)
                elif kind == "y":
                    d, ks = tiles(i)
                    pe.wait_ge(S["rout_odd" if i % 2 else "rout_even"], i // 2 + 1)
                    if i == 0:
                        pe.wait_ge(S["c_copy"], 4)
                    if i == 8:
                        pe.wait_ge(S["yf_copied"], 1)
                    s = i % 4
                    for n, (vv, src, r) in enumerate(((0, X, 0), (1, T, 1), (2, T, 0), (2, X, 1))):
                        for k, kk in enumerate(ks):
                            m, q = kk // 4, slice(32 * (kk % 4), 32 * (kk % 4) + 32)
                            ins = mm(banks[2 + m // 2][q, SEQ * (m % 2):SEQ * (m % 2) + SEQ],
                                     CT[:, d, vv, kk].rearrange("p g c -> p (g c)"), src[s][:, k, r, :], start=n == 0, stop=n == 3)
                    ins.then_inc(S["ssm_y"], 1)
                elif kind == "qkv":
                    c, t = step[1], step[2]
                    j = JOB_QKV[c, t]
                    bank = job_bank(j)
                    for n in ((U_QKV + 2 * c, U_QKV + 2 * c + 1) if c < 4 else (U_QKV + 8,)):
                        loaded(n)
                    for kt in range(KT):
                        if c < 4:
                            o, w = bank[:, :], unit(U_QKV + 2 * c + kt // 4)[:, kt % 4, :]
                        else:
                            o, w = bank[:, 0:256], unit(U_QKV + 8)[:, kt, :]
                        ins = mm(o, hT[:, kt, P * t:P * t + P], w, start=kt == 0, stop=kt == KT - 1)
                    ins.then_inc(S["proj_done"], 1)
                elif kind == "qkT":
                    pe.wait_ge(S["qk_ready"], 2)
                    for g in range(3):
                        n = 3 * i + g
                        if n >= 2:
                            pe.wait_ge(S["qkT_copied"], n - 1)
                        for j in range(4):
                            ins = transpose(banks[6 + n % 2][:, P * j:P * j + P], raw[:, i, P * (4 * g + j):P * (4 * g + j + 1)],
                                            ident[:, :])
                        ins.then_inc(S["qkT_done"], 1)
                elif kind == "scores":
                    h, t = i // 2, i % 2
                    pe.wait_ge(S["qkT_copied"], 6)
                    if i >= 1:
                        pe.wait_ge(S["pt_copied"], i)
                    lo = HD * (h % 2)
                    for g in range(3):
                        n = (4 * g + h) // 2
                        o = banks[6][:, SEQ * g:SEQ * g + SEQ] if g < 2 else banks[7][:, 0:SEQ]
                        ins = mm(o, qkT[lo:lo + HD, n, P * t:P * t + P], qkT[lo:lo + HD, 6 + n, :], start=True, stop=True)
                    ins.then_inc(S["scores_done"], 1)
                elif kind == "gate":
                    j = JOB_GATE[i]
                    bank = job_bank(j)
                    c = i // 2
                    loaded(U_GATE + 2 * c)
                    loaded(U_GATE + 2 * c + 1)
                    for m in (2 * i, 2 * i + 1):
                        for kt in range(KT):
                            ins = mm(bank[:, SEQ * (m % 2):SEQ * (m % 2) + SEQ],
                                     unit(U_GATE + 2 * c + kt // 4)[:, kt % 4, P * (m % 4):P * (m % 4) + P], hT[:, kt, :],
                                     start=kt == 0, stop=kt == KT - 1)
                    ins.then_inc(S["proj_done"], 1)
                elif kind == "pt":
                    pe.wait_ge(S["probs_ready"], i + 1)
                    for n in range(6):
                        ins = transpose(banks[6 + n // 4][:, P * (n % 4):P * (n % 4) + P], probs[:, i % 2, P * n:P * n + P], ident[:, :])
                    ins.then_inc(S["pt_done"], 1)
                elif kind == "pv":
                    j = JOB_PV[i]
                    bank = job_bank(j)
                    pe.wait_ge(S["pt_copied"], 2 * i + 2)
                    lo = HD * (i % 2)
                    for n in range(6):
                        g, kt = n // 2, n % 2
                        ins = mm(bank[lo:lo + HD, 0:SEQ], v[:, kt, HD * (4 * g + i):HD * (4 * g + i) + HD], probsT[:, n, :],
                                 start=n == 0, stop=n == 5)
                    ins.then_inc(S["proj_done"], 1)

            loaded(U_AB)
            pe.wait_ge(S["bu_copied"], 2 * NB)
            pe.wait_ge(S["proj_copied"], n_job)
            pe.wait_ge(S["pt_copied"], 8)
            for m in range(KT):
                for kt in range(2):
                    ins = mm(banks[YA_BANK[m // 2]][:, SEQ * (m % 2):SEQ * (m % 2) + SEQ], unit(U_AB)[:, kt, P * m:P * m + P],
                             atT[:, kt, :], start=kt == 0, stop=kt == 1)
                if m % 2:
                    ins.then_inc(S["ya_done"], 1)
            loaded(U_GLU)
            pe.wait_ge(S["z_ready"], 1)
            for m in range(4):
                for kt in range(4):
                    ins = mm(banks[4 + m // 2][:, SEQ * (m % 2):SEQ * (m % 2) + SEQ], unit(U_GLU)[:, kt, P * m:P * m + P],
                             z[:, kt, :], start=kt == 0, stop=kt == 3)
                if m % 2:
                    ins.then_inc(S["glu_done"], 1)
            loaded(U_SB)
            loaded(U_SB + 1)
            pe.wait_ge(S["zg_ready"], 1)
            for m in range(KT):
                for kt in range(4):
                    ins = mm(banks[YS_BANK[m // 2]][:, SEQ * (m % 2):SEQ * (m % 2) + SEQ],
                             unit(U_SB + kt // 2)[:, kt % 2, P * m:P * m + P], zg[:, kt, :], start=kt == 0, stop=kt == 3)
                if m % 2:
                    ins.then_inc(S["ys_done"], 1)
            for kt in range(KT):
                if kt % 2 == 0:
                    loaded(U_OUT + kt // 2)
                    pe.wait_ge(S["mixed_ready"], kt // 2 + 1)
                for n in range(4):
                    t, ch = n // 2, n % 2
                    ins = mm(banks[XO_BANK[n]][:, :], mT[:, kt, P * t:P * t + P],
                             unit(U_OUT + kt // 2)[:, kt % 2, 512 * ch:512 * ch + 512], start=kt == 0, stop=kt == KT - 1)
                    if kt == KT - 1:
                        ins.then_inc(S["xo_done"], 1)
                if kt % 2 and kt < KT - 1:
                    ins.then_inc(S["out_unit_used"], 1)

            pe.wait_ge(S["h2_ready"], TT)
            for b in range(4):
                for kk in range(2):
                    for t in range(TT):
                        ins = transpose(banks[b][:, P * (2 * kk + t):P * (2 * kk + t + 1)],
                                        h2[:, t, P * (2 * b + kk):P * (2 * b + kk + 1)], ident[:, :])
                ins.then_inc(S["h2T_done"], 1)
            pe.wait_ge(S["moe_in"], 16 * 8)
            pe.wait_ge(S["h2T_copied"], 4)
            for t in range(TT):
                for kt in range(KT):
                    mm(banks[4][:, 32 * t:32 * t + 32], h2T[:, kt, P * t:P * t + P], wr[:, kt, :], start=kt == 0, stop=False)
                ins = mm(banks[4][:, 32 * t:32 * t + 32], ones[0:1, :], br_row, start=False, stop=True)
            ins.then_inc(S["logit_done"], 1)
            pe.wait_ge(S["route_ready"], 1)
            mm(banks[4][:, 64:96], tri, chosen[:, 0, :], start=True, stop=True)
            mm(banks[4][:, 96:128], ones, chosen[:, 0, :], start=True, stop=False)
            mm(banks[4][:, 96:128], tri, chosen[:, 1, :], start=False, stop=True)
            mm(banks[4][0:1, 128:160], ones[:, 0:1], chosen[:, 0, :], start=True, stop=False)
            mm(banks[4][0:1, 128:160], ones[:, 0:1], chosen[:, 1, :], start=False, stop=True).then_inc(S["rank_done"], 1)
            pe.wait_ge(S["route_ready"], 2)
            for t in range(TT):
                ins = transpose(banks[5][0:32, P * t:P * t + P], wgt[:, t, :], ident[:, :])
            ins.then_inc(S["wt_done"], 1)
            pe.wait_ge(S["wt_copied"], 1)
            for n in range(4):
                t, ch = n // 2, n % 2
                mm(banks[n][:, :], wT[:, P * t:P * t + P], bdn[:, 512 * ch:512 * ch + 512], start=True, stop=False,
                   skip_group_check=True)

            def gather():
                for kt in range(KT):
                    for t in range(TT):
                        ins = mm(banks[6][:, CAP * kt:CAP * kt + CAP], h2[:, t, P * kt:P * kt + P], G[:, t, :],
                                 start=t == 0, stop=t == TT - 1)
                ins.then_inc(M["gathered"], 1)

            def scatter():
                for t in range(TT):
                    for ch in range(2):
                        ins = mm(banks[2 * t + ch][:, :], SW[:, P * t:P * t + P], ysb[:, 512 * ch:512 * ch + 512], start=False,
                                 stop=False, skip_group_check=True)
                return ins

            def first_rows(p):
                pe.wait_ge(M["onehots"], p * 33 + 1)
                gather()

            def expert(p, i, b):
                n, e = p * EXPERTS + i * 2 + b, i * 2 + b

                def gate_up(kt, ch):
                    for half in range(2):
                        ins = mm(banks[4 + ch][CAP * half:CAP * half + CAP, :], XeT[:, kt, :],
                                 slot(kt)[:, D * half + 512 * ch:D * half + 512 * ch + 512], start=False, stop=kt == KT - 1)
                    return ins

                pe.wait_ge(M["onehots"], p * 33 + e + 1)
                for ch in range(2):
                    for half in range(2):
                        mm(banks[4 + ch][CAP * half:CAP * half + CAP, :], sel,
                           bgu3[:, D * half + 512 * ch:D * half + 512 * ch + 512], start=True, stop=False)
                pe.wait_ge(M["xT"], p * 33 + e + 1)
                for kt in range(KT):
                    pe.wait_ge(slot_full[kt], (n + (pro_loads[kt] + 1)) * 16)
                    ins = gate_up(kt, 0)
                    if kt < KT // 2:
                        gate_up(kt, 1).then_inc(M["unit_used"], 1)
                    if kt == 0 and b == 0:
                        pe.wait_ge(M["y_low"], n + p + 1)
                        pe.wait_ge(M["y_high"], n + p + 1)
                        scatter()
                ins.then_inc(M["half_done"], 1)
                for kt in range(KT // 2, KT):
                    gate_up(kt, 1).then_inc(M["unit_used"], 1)
                pe.wait_ge(M["onehots"], p * 33 + e + 2)
                gather()
                if b == 0:
                    pe.wait_ge(M["gw_ready"], p * PAIRS + i + 1)
                    for t in range(TT):
                        ins = transpose(banks[7][:, P * t:P * t + P], GW[:, t, :, :].rearrange("p u r -> p (u r)"), ident[:, :])
                    ins.then_inc(M["swt"], 1)
                pe.wait_ge(M["xT"], p * 33 + e + 2)
                for kt in range(KT):
                    if kt % 4 == 0:
                        pe.wait_ge(M["act_ready"], 2 * n + kt // 4 + 1)
                    ins = mm(banks[6][:, CAP * kt:CAP * kt + CAP], m_act[:, P * kt:P * kt + P], ident[0:CAP, 0:CAP],
                             start=True, stop=True)
                ins.then_inc(M["act_trans"], 1)
                if b == 0:
                    pe.wait_ge(M["scatter_w"], p * PAIRS + i + 1)
                else:
                    pe.wait_ge(M["y_low"], n + p + 1)
                    pe.wait_ge(M["y_high"], n + p + 1)
                pe.wait_ge(M["actT"], n + 1)
                for kt in range(KT):
                    s = KT + kt // 2
                    if kt % 2 == 0:
                        pe.wait_ge(slot_full[s], (n + (pro_loads[s] + 1)) * 16)
                    w = slot(s)[:, D * (kt % 2):D * (kt % 2) + D]
                    for half in range(2):
                        ins = mm(banks[7][CAP * half:CAP * half + CAP, :], acT[:, kt, :], w[:, 512 * half:512 * half + 512],
                                 start=kt == 0, stop=kt == KT - 1)
                    if kt % 2:
                        ins.then_inc(M["unit_used"], 1)

            first_rows(0)
            pe.wait_ge(S["bias_parts"], 1)
            with pe.Fori(0, PAIRS) as i:
                expert(0, i, 0)
                expert(0, i, 1)
            pe.wait_ge(M["y_low"], EXPERTS + 1)
            pe.wait_ge(M["y_high"], EXPERTS + 1)
            scatter().then_inc(S["acc_done"], 1)
            pe.wait_ge(S["passes_known"], 1)
            fullest = pe.value_load(cnt_int[0:1, 0:1], min_val=0, max_val=SEQ)
            with pe.Fori(1, PASSES) as p:
                with pe.If(fullest > p * CAP):
                    first_rows(p)
                    with pe.Fori(0, PAIRS) as i:
                        expert(p, i, 0)
                        expert(p, i, 1)
                    pe.wait_ge(M["y_low"], p * 33 + 33)
                    pe.wait_ge(M["y_high"], p * 33 + 33)
                    scatter().then_inc(S["acc_done"], 1)
                with pe.Else():
                    pe.nop().then_inc(S["acc_done"], 1)
                pe.nop()


def kernel(**inputs):
    import numpy as np
    import concourse.bacc as bacc
    from concourse.bass_utils import run_bass_kernel_spmd as run

    nc = bacc.Bacc("TRN2", target_bir_lowering=False, num_devices=1)
    arrays, aps = {}, {}
    for name in inputs:
        arrays[name] = np.ascontiguousarray(inputs[name])
    pos = np.arange(SEQ)
    rel = np.abs(pos[:, None] - pos[None, :])
    kept = np.concatenate([rel <= 64, rel % 4 == 0, rel % 16 == 0], 1)
    masks = np.where(kept, 0.0, -1e30).astype(np.float32)
    inv = np.power(np.float32(10000.0), -np.arange(0, HD, 2, dtype=np.float32) / np.float32(HD))
    ang = pos.astype(np.float32)[:, None] * inv[None, :]
    rope = np.concatenate([np.cos(ang), np.sin(ang)], 1).astype(np.float32)
    tiled = lambda m: np.ascontiguousarray(m.reshape(TT, P, -1).transpose(1, 0, 2))
    const_arrays = {
        "ident": np.eye(P, dtype=np.float32),
        "tri": np.triu(np.ones((P, P), np.float32), 1),
        "iota": np.tile(np.arange(CAP, dtype=np.float32), (P, 1)),
        "pick": np.concatenate([np.tile(np.eye(EXPERTS, dtype=np.float32), (3, 1)), np.zeros((96, 16), np.float32)], 1),
        "iota32": np.tile(np.arange(EXPERTS, dtype=np.float32), (P, 1)),
        "rope": tiled(rope),
        "masks": tiled(masks),
    }
    for name, m in arrays.items():
        aps[name] = nc.dram_tensor(name, m.shape, mybir.dt.from_np(m.dtype), kind="ExternalInput").ap()
    consts = {}
    for name, m in const_arrays.items():
        arrays["const_" + name] = m
        consts[name] = nc.dram_tensor("const_" + name, m.shape, F32, kind="ExternalInput").ap()
    out = nc.dram_tensor("out", [1, SEQ, D], F32, kind="ExternalOutput").ap()
    build(nc, aps, consts, out)
    return run(nc, [arrays], core_ids=[0]).results[0]["out"]
```
